# Optimizing a Trainium2 kernel written in Bass

```python
import math
import numpy as np
import jax
import jax.numpy as jnp
from jax import lax

D_MODEL = 1024
BATCH = 1
SEQ = 512
DEPTH = 2

N_MIXERS = 3
D_FF = 2816
LN_EPS = 1e-5
ALPHA = (2 * DEPTH) ** 0.25
BETA = (8 * DEPTH) ** -0.25
GRID_W = 64
NA_HEADS = 16
NA_HEAD_DIM = D_MODEL // NA_HEADS
NA_ROWS = 8
NA_COLS = 16
NA_QB = 16
HGRN_HEAD_DIM = 128
HGRN_HEADS = D_MODEL // HGRN_HEAD_DIM
HGRN_CHUNK = 64
S5_GROUP_CH = 16
S5_STATE = 64
S5_GROUPS = D_MODEL // S5_GROUP_CH
S5_GROUP_BLOCK = 16
N_NA_LAYERS = (DEPTH + N_MIXERS - 1) // N_MIXERS
N_HGRN_LAYERS = (DEPTH + N_MIXERS - 2) // N_MIXERS
N_S5_LAYERS = (DEPTH + N_MIXERS - 3) // N_MIXERS

kernel_name = 'hybrid_na_hgrn2_s5_macaron_deepnorm_encoder'

def _layer_norm(z, g, b, out_dtype):
    z32 = z.astype(jnp.float32)
    mu = jnp.mean(z32, axis=-1, keepdims=True)
    var = jnp.mean(jnp.square(z32 - mu), axis=-1, keepdims=True)
    return ((z32 - mu) * lax.rsqrt(var + LN_EPS) * g + b).astype(out_dtype)

def _modulate(x, mods, k):
    return x * (1 + mods[:, 3 * k + 1, None, :]) + mods[:, 3 * k, None, :]

def _swiglu(h, w_in, w_out):
    a, b = jnp.split(h @ w_in, 2, axis=-1)
    return (jax.nn.silu(a) * b) @ w_out

def _na_column_tables():
    n_cb = GRID_W // NA_QB
    kb_w = NA_QB + NA_COLS
    cb = np.arange(n_cb)
    ks = np.clip(cb * NA_QB - NA_COLS // 2, 0, GRID_W - kb_w)
    key_cols = ks[:, None] + np.arange(kb_w)[None, :]
    q_cols = cb[:, None] * NA_QB + np.arange(NA_QB)[None, :]
    cs = np.clip(q_cols - NA_COLS // 2, 0, GRID_W - NA_COLS)
    kc = key_cols[:, None, :]
    col_mask = (kc >= cs[..., None]) & (kc < cs[..., None] + NA_COLS)
    dc_idx = np.clip(kc - q_cols[..., None] + NA_COLS - 1, 0, 2 * NA_COLS - 2)
    return key_cols, col_mask, dc_idx

def _neighbourhood_attention(h, w_qkv, rpb, w_out):
    bsz, seq, _ = h.shape
    rows = seq // GRID_W
    kh = min(NA_ROWS, rows)
    key_cols, col_mask, dc_idx = _na_column_tables()
    n_cb, kb_w = key_cols.shape
    qkv = (h @ w_qkv).reshape(bsz, rows, GRID_W, 3, NA_HEADS, NA_HEAD_DIM)
    qkv = qkv.transpose(3, 0, 4, 1, 2, 5)
    q = qkv[0] * NA_HEAD_DIM ** -0.5
    k = qkv[1]
    v = qkv[2]
    mask = jnp.asarray(np.broadcast_to(col_mask[:, :, None, :], (n_cb, NA_QB, kh, kb_w)).reshape(n_cb, NA_QB, kh * kb_w))
    dc = jnp.asarray(dc_idx)

    def row_block(r):
        rs = jnp.clip(r - kh // 2, 0, rows - kh)
        k_rows = lax.dynamic_slice_in_dim(k, rs, kh, axis=2)
        v_rows = lax.dynamic_slice_in_dim(v, rs, kh, axis=2)
        k_blk = k_rows[:, :, :, key_cols].transpose(0, 1, 3, 2, 4, 5).reshape(bsz, NA_HEADS, n_cb, kh * kb_w, NA_HEAD_DIM)
        v_blk = v_rows[:, :, :, key_cols].transpose(0, 1, 3, 2, 4, 5).reshape(bsz, NA_HEADS, n_cb, kh * kb_w, NA_HEAD_DIM)
        q_blk = lax.dynamic_index_in_dim(q, r, axis=2, keepdims=False).reshape(bsz, NA_HEADS, n_cb, NA_QB, NA_HEAD_DIM)
        s = jnp.einsum('bhnqd,bhnkd->bhnqk', q_blk, k_blk).astype(jnp.float32)
        dr_idx = rs + jnp.arange(kh) - r + NA_ROWS - 1
        bias = rpb[:, dr_idx[:, None, None, None], dc[None]]
        bias = bias.transpose(0, 2, 3, 1, 4).reshape(NA_HEADS, n_cb, NA_QB, kh * kb_w).astype(jnp.float32)
        s = jnp.where(mask, s + bias, -jnp.inf)
        p = jax.nn.softmax(s, axis=-1).astype(v.dtype)
        o = jnp.einsum('bhnqk,bhnkd->bhnqd', p, v_blk)
        return o.reshape(bsz, NA_HEADS, GRID_W, NA_HEAD_DIM)

    o = lax.map(row_block, jnp.arange(rows))
    o = o.transpose(1, 0, 3, 2, 4).reshape(bsz, seq, D_MODEL)
    return o @ w_out

def _hgrn_lower_bounds(lb_logits):
    p = jax.nn.softmax(lb_logits.astype(jnp.float32), axis=1)
    cs = jnp.cumsum(p, axis=1)
    return cs - cs[:, :1]

def _gla_chunked(q, k, v, g):
    bsz, seq, nh, dk = q.shape
    dv = v.shape[-1]
    nc = seq // HGRN_CHUNK

    def chunks(t):
        return t.reshape(bsz, nc, HGRN_CHUNK, nh, t.shape[-1]).transpose(1, 0, 3, 2, 4)

    q, k, v, g = chunks(q), chunks(k), chunks(v), chunks(g)
    b = jnp.cumsum(g, axis=3)
    b_ref = b[:, :, :, HGRN_CHUNK // 2:HGRN_CHUNK // 2 + 1]
    b_last = b[:, :, :, -1:]
    tri = jnp.tril(jnp.ones((HGRN_CHUNK, HGRN_CHUNK), dtype=bool))
    a = jnp.einsum('nbhtd,nbhsd->nbhts', q * jnp.exp(b - b_ref), k * jnp.exp(b_ref - b))
    a = jnp.where(tri, a, 0.0)
    o_intra = jnp.einsum('nbhts,nbhsv->nbhtv', a, v)
    q_dec = q * jnp.exp(b)
    k_dec = k * jnp.exp(b_last - b)
    decay = jnp.exp(b_last[:, :, :, 0])

    def step(state, inp):
        qd, kd, vc, dcy = inp
        o = jnp.einsum('bhtd,bhdv->bhtv', qd, state)
        state = dcy[..., None] * state + jnp.einsum('bhsd,bhsv->bhdv', kd, vc)
        return state, o

    state0 = jnp.zeros((bsz, nh, dk, dv), jnp.float32)
    _, o_inter = lax.scan(step, state0, (q_dec, k_dec, v, decay))
    return (o_intra + o_inter).transpose(1, 0, 3, 2, 4).reshape(bsz, seq, nh, dv)

def _hgrn2_mixer(h, w_in, lb_fwd, lb_bwd, norm_g, w_out):
    bsz, seq, _ = h.shape
    shp = (bsz, seq, HGRN_HEADS, HGRN_HEAD_DIM)
    q, i_in, f_fwd, f_bwd, gate = jnp.split(h @ w_in, 5, axis=-1)
    q = jax.nn.silu(q).reshape(shp).astype(jnp.float32)
    v = i_in.reshape(shp).astype(jnp.float32)

    def gates(f_logit, lb):
        lb = lb.reshape(HGRN_HEADS, HGRN_HEAD_DIM)
        f = lb + (1 - lb) * jax.nn.sigmoid(f_logit.reshape(shp).astype(jnp.float32))
        return 1 - f, jnp.log(f)

    k_f, g_f = gates(f_fwd, lb_fwd)
    o_f = _gla_chunked(q, k_f, v, g_f)
    k_b, g_b = gates(f_bwd, lb_bwd)
    o_b = jnp.flip(_gla_chunked(jnp.flip(q, 1), jnp.flip(k_b, 1), jnp.flip(v, 1), jnp.flip(g_b, 1)), 1)
    o = o_f + o_b
    o = o * lax.rsqrt(jnp.mean(jnp.square(o), axis=-1, keepdims=True) + LN_EPS)
    o = o.reshape(bsz, seq, D_MODEL) * norm_g * jax.nn.silu(gate.astype(jnp.float32))
    return o.astype(h.dtype) @ w_out

def _complex_affine_combine(e1, e2):
    a1r, a1i, b1r, b1i = e1
    a2r, a2i, b2r, b2i = e2
    return (a2r * a1r - a2i * a1i,
            a2r * a1i + a2i * a1r,
            a2r * b1r - a2i * b1i + b2r,
            a2r * b1i + a2i * b1r + b2i)

def _s5_scan(bu_re, bu_im, a_re, a_im, log_dt, reverse):
    a_re = a_re.astype(jnp.float32)
    a_im = a_im.astype(jnp.float32)
    dt = jnp.exp(log_dt.astype(jnp.float32))[:, None]
    mag = jnp.exp(a_re * dt)
    ang = a_im * dt
    ab_re = mag * jnp.cos(ang)
    ab_im = mag * jnp.sin(ang)
    den = a_re * a_re + a_im * a_im
    z_re = ((ab_re - 1) * a_re + ab_im * a_im) / den
    z_im = (ab_im * a_re - (ab_re - 1) * a_im) / den
    bb_re = z_re * bu_re - z_im * bu_im
    bb_im = z_re * bu_im + z_im * bu_re
    seq = bu_re.shape[0]
    lam_re = jnp.broadcast_to(ab_re, (seq, 1) + ab_re.shape)
    lam_im = jnp.broadcast_to(ab_im, (seq, 1) + ab_im.shape)
    _, _, x_re, x_im = lax.associative_scan(_complex_affine_combine, (lam_re, lam_im, bb_re, bb_im), reverse=reverse, axis=0)
    return x_re, x_im

def _s5_mixer(h, a_re, a_im, log_dt, b_re, b_im, c_re, c_im, d_skip, w_out):
    bsz, seq, _ = h.shape
    nb = S5_GROUPS // S5_GROUP_BLOCK
    u = h.astype(jnp.float32).reshape(bsz, seq, nb, S5_GROUP_BLOCK, S5_GROUP_CH).transpose(2, 1, 0, 3, 4)
    a_re_b = a_re.reshape(2, nb, S5_GROUP_BLOCK, S5_STATE).transpose(1, 0, 2, 3)
    a_im_b = a_im.reshape(2, nb, S5_GROUP_BLOCK, S5_STATE).transpose(1, 0, 2, 3)
    ldt_b = log_dt.reshape(2, nb, S5_GROUP_BLOCK).transpose(1, 0, 2)
    b_re_b = b_re.reshape(nb, S5_GROUP_BLOCK, S5_STATE, S5_GROUP_CH)
    b_im_b = b_im.reshape(nb, S5_GROUP_BLOCK, S5_STATE, S5_GROUP_CH)
    c_re_b = c_re.reshape(nb, S5_GROUP_BLOCK, S5_GROUP_CH, S5_STATE)
    c_im_b = c_im.reshape(nb, S5_GROUP_BLOCK, S5_GROUP_CH, S5_STATE)
    d_b = d_skip.reshape(nb, S5_GROUP_BLOCK, S5_GROUP_CH)

    def group_block(args):
        u_b, ar, ai, ldt, br, bi, cr, ci, dd = args
        bu_re = jnp.einsum('sbgc,gpc->sbgp', u_b, br.astype(jnp.float32))
        bu_im = jnp.einsum('sbgc,gpc->sbgp', u_b, bi.astype(jnp.float32))
        xf_re, xf_im = _s5_scan(bu_re, bu_im, ar[0], ai[0], ldt[0], False)
        xb_re, xb_im = _s5_scan(bu_re, bu_im, ar[1], ai[1], ldt[1], True)
        x_re = xf_re + xb_re
        x_im = xf_im + xb_im
        y = jnp.einsum('sbgp,gcp->sbgc', x_re, cr.astype(jnp.float32)) - jnp.einsum('sbgp,gcp->sbgc', x_im, ci.astype(jnp.float32))
        return y + dd * u_b

    y = lax.map(group_block, (u, a_re_b, a_im_b, ldt_b, b_re_b, b_im_b, c_re_b, c_im_b, d_b))
    y = y.transpose(2, 1, 0, 3, 4).reshape(bsz, seq, D_MODEL)
    y = jax.nn.gelu(y).astype(h.dtype)
    val, gte = jnp.split(y @ w_out, 2, axis=-1)
    return val * jax.nn.sigmoid(gte)

def setup_inputs(seed: int = 0) -> dict:
    key = jax.random.key(seed)
    ks = jax.random.split(key, 24)
    d = D_MODEL

    def nrm(k, shape, s):
        return jax.random.normal(k, shape, jnp.float32) * s

    s5_shape = (N_S5_LAYERS, 2, S5_GROUPS, S5_STATE)
    n_idx = jnp.arange(S5_STATE, dtype=jnp.float32)
    return {
        'x': nrm(ks[0], (BATCH, SEQ, d), 1.0),
        'c': nrm(ks[1], (BATCH, d), 1.0),
        'ada_w': nrm(ks[2], (DEPTH, d, 9 * d), d ** -0.5),
        'ada_b': nrm(ks[3], (DEPTH, 9 * d), 0.01),
        'ln_g': 1.0 + nrm(ks[4], (DEPTH, 3, d), 0.01),
        'ln_b': nrm(ks[5], (DEPTH, 3, d), 0.01),
        'ffn_w_in': nrm(ks[6], (DEPTH, 2, d, 2 * D_FF), d ** -0.5),
        'ffn_w_out': nrm(ks[7], (DEPTH, 2, D_FF, d), BETA * D_FF ** -0.5),
        'na_w_qkv': nrm(ks[8], (N_NA_LAYERS, d, 3 * d), d ** -0.5),
        'na_rpb': nrm(ks[9], (N_NA_LAYERS, NA_HEADS, 2 * NA_ROWS - 1, 2 * NA_COLS - 1), 0.1),
        'na_w_out': nrm(ks[10], (N_NA_LAYERS, d, d), BETA * d ** -0.5),
        'hgrn_w_in': nrm(ks[11], (N_HGRN_LAYERS, d, 5 * d), d ** -0.5),
        'hgrn_lb_logits': nrm(ks[12], (2, DEPTH, d), 0.1),
        'hgrn_norm_g': 1.0 + nrm(ks[13], (N_HGRN_LAYERS, d), 0.01),
        'hgrn_w_out': nrm(ks[14], (N_HGRN_LAYERS, d, d), BETA * d ** -0.5),
        's5_a_re': -0.5 + nrm(ks[15], s5_shape, 0.01),
        's5_a_im': math.pi * n_idx + nrm(ks[16], s5_shape, 0.01),
        's5_log_dt': jax.random.uniform(ks[17], (N_S5_LAYERS, 2, S5_GROUPS), jnp.float32, math.log(1e-3), math.log(1e-1)),
        's5_b_re': nrm(ks[18], (N_S5_LAYERS, S5_GROUPS, S5_STATE, S5_GROUP_CH), (2 * S5_GROUP_CH) ** -0.5),
        's5_b_im': nrm(ks[19], (N_S5_LAYERS, S5_GROUPS, S5_STATE, S5_GROUP_CH), (2 * S5_GROUP_CH) ** -0.5),
        's5_c_re': nrm(ks[20], (N_S5_LAYERS, S5_GROUPS, S5_GROUP_CH, S5_STATE), S5_STATE ** -0.5),
        's5_c_im': nrm(ks[21], (N_S5_LAYERS, S5_GROUPS, S5_GROUP_CH, S5_STATE), S5_STATE ** -0.5),
        's5_d': nrm(ks[22], (N_S5_LAYERS, d), 1.0),
        's5_w_out': nrm(ks[23], (N_S5_LAYERS, d, 2 * d), BETA * d ** -0.5),
    }

def reference(x, c, ada_w, ada_b, ln_g, ln_b, ffn_w_in, ffn_w_out, na_w_qkv, na_rpb, na_w_out,
              hgrn_w_in, hgrn_lb_logits, hgrn_norm_g, hgrn_w_out,
              s5_a_re, s5_a_im, s5_log_dt, s5_b_re, s5_b_im, s5_c_re, s5_c_im, s5_d, s5_w_out):
    dtype = x.dtype
    bsz = x.shape[0]
    lbs = _hgrn_lower_bounds(hgrn_lb_logits)
    for i in range(DEPTH):
        kind = i % N_MIXERS
        j = i // N_MIXERS
        mods = (jax.nn.silu(c) @ ada_w[i] + ada_b[i]).reshape(bsz, 9, D_MODEL)
        h = _modulate(x, mods, 0)
        y = _swiglu(h, ffn_w_in[i, 0], ffn_w_out[i, 0])
        x = _layer_norm(ALPHA * x + 0.5 * mods[:, 2, None, :] * y, ln_g[i, 0], ln_b[i, 0], dtype)
        h = _modulate(x, mods, 1)
        if kind == 0:
            y = _neighbourhood_attention(h, na_w_qkv[j], na_rpb[j], na_w_out[j])
        elif kind == 1:
            y = _hgrn2_mixer(h, hgrn_w_in[j], lbs[0, i], lbs[1, i], hgrn_norm_g[j], hgrn_w_out[j])
        else:
            y = _s5_mixer(h, s5_a_re[j], s5_a_im[j], s5_log_dt[j], s5_b_re[j], s5_b_im[j],
                          s5_c_re[j], s5_c_im[j], s5_d[j], s5_w_out[j])
        x = _layer_norm(ALPHA * x + mods[:, 5, None, :] * y, ln_g[i, 1], ln_b[i, 1], dtype)
        h = _modulate(x, mods, 2)
        y = _swiglu(h, ffn_w_in[i, 1], ffn_w_out[i, 1])
        x = _layer_norm(ALPHA * x + 0.5 * mods[:, 8, None, :] * y, ln_g[i, 2], ln_b[i, 2], dtype)
    return x


_drawn_inputs = setup_inputs


def setup_inputs(seed=0):
    import zlib

    import numpy as np

    out = dict(_drawn_inputs(seed))
    spreads = {}
    factors = {'ada_b': 7.337, 'na_rpb': 8.0, 'hgrn_lb_logits': 8.0, 'hgrn_norm_g': 8.0}
    for name, (base, spread) in spreads.items():
        noise = np.random.default_rng([zlib.crc32(name.encode()), seed]).standard_normal(out[name].shape)
        drawn = base * np.exp(spread * noise) if base else spread * noise
        out[name] = jnp.asarray(drawn.astype(out[name].dtype))
    for name, factor in factors.items():
        out[name] = (out[name] * factor).astype(out[name].dtype)
    return out
```

```python
from contextlib import ExitStack

import concourse.bass as bass
from concourse import mybir



class Phase:
    def __init__(self, kind, iters, body, kt, ffn=None, layer=None, sub=None, half=None, tile0=0, mixer=None, last=False,
                 per_tile=1, ln=None):
        self.kind, self.iters, self.body, self.kt = kind, iters, body, kt
        self.ffn, self.layer, self.sub, self.half, self.tile0 = ffn, layer, sub, half, tile0
        self.mixer, self.last, self.per_tile, self.ln = mixer, last, per_tile, ln
        self.ada = None


class AdaRide:
    def __init__(self, slot0, first):
        self.slot0, self.first = slot0, first


P = 128
ALU = mybir.AluOpType
ACT = mybir.ActivationFunctionType
F32 = mybir.dt.float32
F32R = mybir.dt.float32r
BF16 = mybir.dt.bfloat16
U8 = mybir.dt.uint8
NEG = -3.0e38

T = 512
D = 1024
KT = D // P
F = 2816
FT = F // P
LAYERS = 2
MODS = 9
EPS = 1e-5
ALPHA = (2 * LAYERS) ** 0.25
GRID = 64
ROWS = T // GRID
NA_HEADS = 16
HD = D // NA_HEADS
QB = 16
CB = GRID // QB
KW = 32
KEYS = ROWS * KW
KEY_START = [0, 8, 24, 32]
VARIANT = [0, 1, 1, 2]
SHIFT = [16, 8, 0]
RPB_R, RPB_C = 15, 31
TAB_C = 64
HEADS = 8
CH = 64
NCH = T // CH
HALF_PAIRS = [12, 10]
NLN = 6


class Semaphores:
    def __init__(self, sem):
        self.w_hi_done = sem("w_hi_done")
        self.w_lo_done = sem("w_lo_done")
        self.unit_done = sem("unit_done")
        self.pair_free = sem("pair_free")
        self.silu_done = sem("silu_done")
        self.g32_done = sem("g32_done")
        self.g_hi_done = sem("g_hi_done")
        self.g_ready = sem("g_ready")
        self.y_read = sem("y_read")
        self.x_copied = sem("x_copied")
        self.zsum_done = sem("zsum_done")
        self.sq_done = sem("sq_done")
        self.qsum_done = sem("qsum_done")
        self.zeroed = sem("zeroed")
        self.stat_done = sem("stat_done")
        self.mean2_done = sem("mean2_done")
        self.var1_done = sem("var1_done")
        self.var_done = sem("var_done")
        self.sd_done = sem("sd_done")
        self.rstd_done = sem("rstd_done")
        self.cent_done = sem("cent_done")
        self.norm_done = sem("norm_done")
        self.h_hi_done = sem("h_hi_done")
        self.h_ready = sem("h_ready")
        self.x_ready = sem("x_ready")
        self.const_done = sem("const_done")
        self.small_in = sem("small_in")
        self.vec_mm = sem("vec_mm")
        self.vec_done = sem("vec_done")
        self.silu_c = sem("silu_c")
        self.lb_act = sem("lb_act")
        self.cols = sem("cols")
        self.x_loaded = sem("x_loaded")
        self.xt_mm = sem("xt_mm")
        self.xt_done = sem("xt_done")
        self.ada_step = sem("ada_step")
        self.acc_out_ready = sem("acc_out_ready")
        self.ada_reduced = sem("ada_reduced")
        self.fin_done = sem("fin_done")
        self.fin_mm = sem("fin_mm")
        self.fin_left = sem("fin_left")
        self.fin_right = sem("fin_right")
        self.out_done = sem("out_done")
        self.tab_zero = sem("tab_zero")
        self.tab_init = sem("tab_init")
        self.tab_in = sem("tab_in")
        self.bias_done = sem("bias_done")
        self.mask_done = sem("mask_done")
        self.q_ready = sem("q_ready")
        self.k_ready = sem("k_ready")
        self.v_ready = sem("v_ready")
        self.vkey_mm = sem("vkey_mm")
        self.vkey_ready = sem("vkey_ready")
        self.s_mm = sem("s_mm")
        self.bias_add = sem("bias_add")
        self.neg_done = sem("neg_done")
        self.exp_done = sem("exp_done")
        self.inv_done = sem("inv_done")
        self.p_ready = sem("p_ready")
        self.pt_mm = sem("pt_mm")
        self.pt_ready0 = sem("pt_ready0")
        self.pt_ready1 = sem("pt_ready1")
        self.pv_mm = sem("pv_mm")
        self.o_copied = sem("o_copied")
        self.o_hi_done = sem("o_hi_done")
        self.o_ready = sem("o_ready")
        self.ev_done = sem("ev_done")
        self.qs_done = sem("qs_done")
        self.gs_done = sem("gs_done")
        self.vtok_mm = sem("vtok_mm")
        self.vtok_ready = sem("vtok_ready")
        self.f_done = sem("f_done")
        self.k1_done = sem("k1_done")
        self.lg_done = sem("lg_done")
        self.cum_done = sem("cum_done")
        self.dd_done = sem("dd_done")
        self.e1_done = sem("e1_done")
        self.e2_done = sem("e2_done")
        self.gs1_done = sem("gs1_done")
        self.gs2_done = sem("gs2_done")
        self.gam_done = sem("gam_done")
        self.qq_done = sem("qq_done")
        self.kk_done = sem("kk_done")
        self.qg_done = sem("qg_done")
        self.a_mm = sem("a_mm")
        self.am_ready = sem("am_ready")
        self.kkt_mm = sem("kkt_mm")
        self.kkt_ready = sem("kkt_ready")
        self.pp_mm = sem("pp_mm")
        self.st_done = sem("st_done")
        self.inter_mm = sem("inter_mm")
        self.osq_done = sem("osq_done")
        self.ms_mm = sem("ms_mm")
        self.lnv_done = sem("lnv_done")
        self.hrstd_done = sem("hrstd_done")
        self.n1_done = sem("n1_done")
        self.n2_done = sem("n2_done")
        self.hhi_done = sem("hhi_done")
        self.ho_ready = sem("ho_ready")
        self.hconst = sem("hconst")
        self.am_zero = sem("am_zero")
        self.w_loaded = [sem(f"w_loaded{s}") for s in range(5)]
        self.boot_loaded = [sem(f"boot_loaded{s}") for s in range(7)]
        self.ada_loaded = [sem(f"ada_loaded{s}") for s in range(2)]
        self.tab_loaded = [sem(f"tab_loaded{s}") for s in range(2)]


def plan_phases():
    phases = []

    def add(**k):
        phases.append(Phase(**k))

    for ffn in range(4):
        layer, sub = ffn // 2, ffn % 2
        for half, pairs in enumerate(HALF_PAIRS):
            add(kind="in", ffn=ffn, layer=layer, sub=sub, half=half, iters=pairs // 2, body=4, kt=KT, tile0=half * HALF_PAIRS[0])
            add(kind="out", ffn=ffn, layer=layer, sub=sub, half=half, iters=KT // 2, body=4, kt=pairs // 2, tile0=half * HALF_PAIRS[0],
                last=half == 1, per_tile=2, ln=[0, 2, 3, 5][ffn])
        if ffn == 0:
            add(kind="na", iters=NA_HEADS // 2, body=3, kt=KT)
            add(kind="out", ffn=None, mixer="na", iters=KT // 4, body=4, kt=KT, last=True, per_tile=1, ln=1)
        if ffn == 2:
            add(kind="hg", iters=HEADS, body=5, kt=KT)
            add(kind="out", ffn=None, mixer="hg", iters=KT // 4, body=4, kt=KT, last=True, per_tile=1, ln=4)
    phases[0].ada = AdaRide(slot0=2, first=[(0, 2 + i) for i in range(6)])
    phases[2].ada = AdaRide(slot0=8, first=[(1, i) for i in range(4)] + [(0, 8)])
    phases[8].ada = AdaRide(slot0=13, first=[(1, 4 + i) for i in range(5)])
    unit = pair = otile = stat = 0
    uses, last_user = [0] * 5, [None] * 5
    for n, ph in enumerate(phases):
        ph.n = n
        ph.u0, ph.p0, ph.y0, ph.t0 = unit, pair, otile, stat
        ph.uses, ph.last_user = list(uses), list(last_user)
        for s in range(ph.body):
            uses[s] += ph.iters
            last_user[s] = unit + (ph.iters - 1) * ph.body + s
        unit += ph.iters * ph.body
        if ph.kind == "in":
            pair += 2 * ph.iters
        if ph.kind == "out":
            otile += KT
            if ph.last:
                stat += KT
    phases[-1].units = unit
    return phases


def build(nc, x_in, c_in, ada_w, ada_b, ln_g, ln_b, ffn_w_in, ffn_w_out, na_w_qkv, na_rpb, na_w_out,
          hgrn_w_in, hgrn_lb_logits, hgrn_norm_g, hgrn_w_out, out):
    phases = plan_phases()
    ctx = ExitStack()
    with ctx:
        def sb(name, shape, dt=F32, where=ctx):
            return where.enter_context(nc.sbuf_tensor(name, shape, dt))

        x = sb("x", [P, KT, T])
        h_hi = sb("h_hi", [P, KT, T], F32R)
        h_lo = sb("h_lo", [P, KT, T], F32R)
        raw = [sb(f"raw{s}", [P, KT, P]) for s in range(4)]
        w_hi = [sb(f"w_hi{s}", [P, KT, P], F32R) for s in range(4)]
        w_lo = [sb(f"w_lo{s}", [P, KT, P], F32R) for s in range(4)]
        zt = [sb(f"zt{i}", [P, T]) for i in range(2)]
        sq = sb("sq", [P, T])
        zsum = sb("zsum", [P, T])
        qsum = sb("qsum", [P, T])
        rstd = sb("rstd", [P, T])
        var = sb("var", [P, T])
        mean2 = sb("mean2", [P, T])
        h32 = [sb(f"h32_{i}", [P, T]) for i in range(2)]
        ident = sb("ident", [P, P])
        mean_w = sb("mean_w", [P, P])
        head_w = sb("head_w", [P, P])
        one = sb("one", [P, 1])
        eps_col = sb("eps_col", [P, 1])
        vec = sb("vec", [P, 3, P])
        c_silu = sb("c_silu", [P, KT])
        mods = sb("mods", [P, LAYERS, MODS, KT])
        A = sb("A", [P, NLN, KT])
        B = sb("B", [P, NLN, KT])
        M = sb("M", [P, NLN, KT])
        AG = sb("AG", [P, NLN, KT])
        AB = sb("AB", [P, NLN, KT])
        lb = sb("lb", [P, 2, KT])
        lb1 = sb("lb1", [P, 2, KT])
        small = sb("small", [P, 4, 2 * KT])

        reg = ExitStack()
        with reg:
            x_tok = sb("x_tok", [P, T // P, D], where=reg)
            boot = [sb(f"boot{i}", [P, D], where=reg) for i in range(7)]
            vrow = sb("vrow", [P, 3, P], where=reg)
        reg = ExitStack()
        with reg:
            g_hi = sb("g_hi", [P, HALF_PAIRS[0], T], F32R, where=reg)
            g_lo = sb("g_lo", [P, HALF_PAIRS[0], T], F32R, where=reg)
            s_tmp = [sb(f"s_tmp{i}", [P, T], where=reg) for i in range(2)]
            g32 = [sb(f"g32_{i}", [P, T], where=reg) for i in range(2)]
            ada_raw = [sb(f"ada_raw{i}", [P, D], where=reg) for i in range(2)]
            acc = sb("acc", [P, D], where=reg)
            acc_out = sb("acc_out", [P, D], where=reg)
        reg = ExitStack()
        with reg:
            ona_hi = sb("ona_hi", [P, KT, T], F32R, where=reg)
            ona_lo = sb("ona_lo", [P, KT, T], F32R, where=reg)
            q_sb = sb("q_sb", [P, GRID, ROWS], where=reg)
            k_sb = sb("k_sb", [P, ROWS, GRID], where=reg)
            v_win = sb("v_win", [P, CB, ROWS, KW], where=reg)
            v_key = sb("v_key", [P, CB * 2, P], where=reg)
            tab = [sb(f"tab{i}", [P, ROWS, TAB_C], where=reg) for i in range(2)]
            bias = [sb(f"bias{i}", [P, 3, KEYS], where=reg) for i in range(2)]
            p_sb = [sb(f"p_sb{i}", [P, CB, KEYS], where=reg) for i in range(2)]
            p_key = [sb(f"p_key{i}", [P, CB * 2, P], where=reg) for i in range(2)]
            mask = sb("mask", [P, 3, ROWS, KW], where=reg)
            gate = sb("gate", [P, 2], where=reg)
            p_max = [sb(f"p_max{i}", [P, CB], where=reg) for i in range(2)]
            p_neg = [sb(f"p_neg{i}", [P, CB], where=reg) for i in range(2)]
            p_sum = [sb(f"p_sum{i}", [P, CB], where=reg) for i in range(2)]
            p_inv = [sb(f"p_inv{i}", [P, CB], where=reg) for i in range(2)]
        reg = ExitStack()
        with reg:
            ohg_hi = sb("ohg_hi", [P, KT, T], F32R, where=reg)
            ohg_lo = sb("ohg_lo", [P, KT, T], F32R, where=reg)
            raw.append(sb("raw4", [P, KT, P], where=reg))
            w_hi.append(sb("w_hi4", [P, KT, P], F32R, where=reg))
            w_lo.append(sb("w_lo4", [P, KT, P], F32R, where=reg))
            q_raw = sb("q_raw", [P, T], where=reg)
            q_sig = sb("q_sig", [P, T], where=reg)
            v_raw = sb("v_raw", [P, T], where=reg)
            f_sig = [sb(f"f_sig{d}", [P, T], where=reg) for d in range(2)]
            gt_raw = sb("gt_raw", [P, T], where=reg)
            gt_sig = sb("gt_sig", [P, T], where=reg)
            kk = [zt[0], zt[1]]
            lg = [sb(f"lg{d}", [P, T], where=reg) for d in range(2)]
            cum = [sb(f"cum{d}", [P, T], where=reg) for d in range(2)]
            e1 = [sb(f"e1_{d}", [P, T], where=reg) for d in range(2)]
            am = [sb(f"am{d}", [P, T], where=reg) for d in range(2)]
            st = [sb(f"st{d}", [P, NCH - 1, P], where=reg) for d in range(2)]
            gam = [sb(f"gam{d}", [P, NCH], where=reg) for d in range(2)]
            gam_t = [sb(f"gam_t{d}", [P, NCH], where=reg) for d in range(2)]
            keep = [sb(f"keep{d}", [P, T], BF16, where=reg) for d in range(2)]
            tri = [sb(f"tri{d}", [P, P], U8, where=reg) for d in range(2)]
            tri_f = sb("tri_f", [P, P], where=reg)
            v_tok = h32[0]
            kk_tok = [f_sig[0], f_sig[1]]

        table = nc.dram_tensor("bias_rows", [NA_HEADS, RPB_R + 1, TAB_C], F32)

        ps = ctx.enter_context(nc.psum_tensor("ps", [P, 8, 512], F32))

        S = Semaphores(lambda name: ctx.enter_context(nc.semaphore(name)))

        block = ctx.enter_context(nc.Block())

        win = ffn_w_in.rearrange("l s (k p) n -> l s p k n", p=P)
        wqkv = na_w_qkv.rearrange("l (k p) n -> l p k n", p=P)
        wna = na_w_out.rearrange("l (k p) n -> l p k n", p=P)
        whg = hgrn_w_in.rearrange("l (k p) n -> l p k n", p=P)
        whgo = hgrn_w_out.rearrange("l (k p) n -> l p k n", p=P)
        wout = ffn_w_out.rearrange("l s (k p) n -> l s p k n", p=P)
        ada = ada_w.rearrange("l (k p) n -> l k p n", p=P)

        def unit_of(ph, i, s):
            return ph.u0 + ph.body * i + s

        def source(ph, i, s):
            if ph.kind == "in":
                col = (ph.tile0 + s // 2) * P + (F if s % 2 else 0)
                return win[ph.layer, ph.sub, :, :, bass.ds(i * (2 * P) + col, P)]
            if ph.kind == "na":
                return wqkv[0, :, :, bass.ds(i * P + s * D, P)]
            if ph.kind == "hg":
                return whg[0, :, :, bass.ds(i * P + s * D, P)]
            if ph.ffn is None:
                w = wna if ph.mixer == "na" else whgo
                return w[0, :, :, bass.ds(i * (4 * P) + s * P, P)]
            k0 = ph.tile0 + (s % 2) * ph.kt
            return wout[ph.layer, ph.sub, :, k0:k0 + ph.kt, bass.ds(i * (2 * P) + (s // 2) * P, P)]

        def slot_free(eng, sem, ph, i, s):
            if isinstance(i, int) and i == 0:
                if ph.last_user[s] is not None:
                    eng.wait_ge(sem, ph.last_user[s] + 1)
            else:
                eng.wait_ge(sem, unit_of(ph, i, s) - ph.body + 1)

        def lot(ph, i, s):
            return i * 16 + 16 * (ph.uses[s] + 1)

        def drive(eng, convert, finish, end, after, ride=None):
            for n, ph in enumerate(phases):
                with eng.Fori(1, ph.iters) as i:
                    for s in range(ph.body):
                        convert(ph, i, s)
                        finish(ph, i - 1, s)
                        if ride is not None and ph.ada is not None:
                            ride(ph, i, s)
                    end(ph, i - 1)
                nxt = phases[n + 1] if n + 1 < len(phases) else None
                for s in range(max(ph.body, 4)):
                    if nxt is not None and s < min(nxt.body, 4):
                        convert(nxt, 0, s)
                    if s < ph.body:
                        finish(ph, ph.iters - 1, s)
                    if ride is not None and nxt is not None and nxt.ada is not None and s < 4:
                        ride(nxt, 0, s)
                end(ph, ph.iters - 1)
                after(ph)
                if nxt is not None and nxt.body == 5:
                    convert(nxt, 0, 4)

        def ph_h(ph):
            return [0, 2, 3, 5][ph.ffn]

        def g_base(ph):
            return phases[ph.n - 1].p0


        @block.sync
        def _(sp):
            def load(ph, i, s):
                slot_free(sp, S.w_lo_done, ph, i, s)
                if ph.kind == "hg" and s == 4 and isinstance(i, int):
                    sp.wait_ge(S.unit_done, ph.u0)
                sp.dma_start(raw[s][:, 0:ph.kt, :], source(ph, i, s)).then_inc(S.w_loaded[s], 16)

            def ada_loads(ph, i, s, at):
                layer, m = at
                for k in (2 * s, 2 * s + 1):
                    sp.wait_ge(S.ada_step, (i + ph.ada.slot0) * 8 + k - 1)
                    sp.dma_start(ada_raw[k % 2][:], ada[layer, k, :, bass.ds(m * D, D)]).then_inc(S.ada_loaded[k % 2], 16)

            def tab_loads(i):
                for hp in range(2):
                    if not isinstance(i, int):
                        sp.wait_ge(S.bias_done, i * 2 + hp - 1)
                    sp.dma_start(tab[hp][:].rearrange("p a b -> p (a b)"),
                                 bass.AP(tensor=table, offset=i * (2 * (RPB_R + 1) * TAB_C) + hp * (RPB_R + 1) * TAB_C,
                                         ap=[[1, QB], [TAB_C, ROWS], [1, ROWS * TAB_C]])).then_inc(S.tab_loaded[hp], 16)

            sp.dma_start(vrow[0:72, 0, :], ada_b[0].rearrange("(r p) -> r p", p=P)).then_inc(S.small_in, 16)
            sp.dma_start(vrow[0:72, 1, :], ada_b[1].rearrange("(r p) -> r p", p=P)).then_inc(S.small_in, 16)
            sp.dma_start(vrow[72:120, 0, :], ln_g.rearrange("l s (r p) -> (l s r) p", p=P)).then_inc(S.small_in, 16)
            sp.dma_start(vrow[72:120, 1, :], ln_b.rearrange("l s (r p) -> (l s r) p", p=P)).then_inc(S.small_in, 16)
            sp.dma_start(vrow[0:8, 2, :], hgrn_norm_g.rearrange("l (r p) -> (l r) p", p=P)).then_inc(S.small_in, 16)
            sp.dma_start(vrow[8:40, 2, :], hgrn_lb_logits.rearrange("a l (r p) -> (a l r) p", p=P)).then_inc(S.small_in, 16)
            sp.dma_start(vrow[40:48, 2, :], c_in.rearrange("b (r p) -> (b r) p", p=P)).then_inc(S.small_in, 16)
            for t in range(T // P):
                sp.dma_start(x_tok[:, t, :], x_in[0, t * P:(t + 1) * P, :]).then_inc(S.x_loaded, 16)
            for k in range(2 * KT):
                if k >= 7:
                    sp.wait_ge(S.ada_step, k - 6)
                sp.dma_start(boot[k % 7][:], ada[0, k % KT, :, (k // KT) * D:(k // KT + 1) * D]).then_inc(S.boot_loaded[k % 7], 16)
                if k in (3, 6, 9, 12):
                    load(phases[0], 0, k // 3 - 1)
            sp.wait_ge(S.tab_zero, 1)
            sp.dma_start(table[:].rearrange("h r c -> (h r) c").rearrange("(a b) c -> a (b c)", b=2), zsum[:, 0:2 * TAB_C]).then_inc(S.tab_init, 16)
            sp.wait_ge(S.tab_init, 16)
            sp.dma_start(table[:, 0:RPB_R, 16:16 + RPB_C], na_rpb[0]).then_inc(S.tab_in, 16)
            sp.wait_ge(S.tab_in, 16)
            for n, ph in enumerate(phases):
                if ph.kind == "na":
                    sp.wait_ge(S.unit_done, ph.u0)
                    tab_loads(0)
                with sp.Fori(1, ph.iters) as i:
                    for s in range(ph.body):
                        load(ph, i, s)
                        if ph.ada is not None:
                            layer, m = ph.ada.first[0]
                            ada_loads(ph, i - 1, s, (layer, i - 1 + m))
                    if ph.kind == "na":
                        tab_loads(i)
                nxt = phases[n + 1] if n + 1 < len(phases) else None
                for s in range(4):
                    if nxt is not None and s < nxt.body:
                        load(nxt, 0, s)
                    if ph.ada is not None:
                        ada_loads(ph, ph.iters - 1, s, ph.ada.first[-1])
                if nxt is not None and nxt.body == 5:
                    load(nxt, 0, 4)
            for t in range(T // P):
                sp.wait_ge(S.fin_left, t + 1)
                sp.wait_ge(S.fin_right, t + 1)
                sp.dma_start(out[0, t * P:(t + 1) * P, :], x_tok[:, t, :]).then_inc(S.out_done, 16)
            sp.wait_ge(S.out_done, 16 * (T // P))

        @block.scalar
        def _(act):
            def convert(ph, i, s):
                act.wait_ge(S.w_loaded[s], lot(ph, i, s))
                slot_free(act, S.unit_done, ph, i, s)
                nc.scalar.activation(w_hi[s][:, 0:ph.kt, :], raw[s][:, 0:ph.kt, :], ACT.Copy).then_inc(S.w_hi_done, 1)

            def finish(ph, i, s):
                if ph.kind == "in" and s % 2 == 1:
                    pair = ph.p0 + s // 2 + i * 2
                    act.wait_ge(S.unit_done, unit_of(ph, i, s) + 1)
                    act.wait_ge(S.pair_free, pair + 1)
                    nc.scalar.activation(s_tmp[s // 2][:], ps[:, s - 1, :], ACT.Silu).then_inc(S.silu_done, 1)
                if ph.kind == "out" and ph.last and s % ph.per_tile == ph.per_tile - 1:
                    j = s // ph.per_tile
                    tile = i * (ph.body // ph.per_tile) + j
                    act.wait_ge(S.y_read, tile + ph.y0 + 3)
                    act.wait_ge(S.qsum_done, tile + ph.t0 + 2)
                    nc.scalar.activation(sq[:], zt[j % 2][:], ACT.Square).then_inc(S.sq_done, 1)
                if ph.kind == "na":
                    act.wait_ge(S.unit_done, unit_of(ph, i, s) + 1)
                    if s == 0:
                        wait_heads(i)
                        nc.scalar.activation(q_sb[:, ::-1, ::-1].rearrange("p c r -> p r c"), ps[:, 0, :].rearrange("p (r c) -> p r c", r=ROWS),
                                             ACT.Copy, scale=HD ** -0.5).then_inc(S.q_ready, 1)
                    if s == 2:
                        if not (isinstance(i, int) and i == 0):
                            act.wait_ge(S.vkey_mm, i)
                        v = ps[:, 2, :].rearrange("p (r c) -> p r c", r=ROWS)
                        for cb in range(CB):
                            k0 = KEY_START[cb]
                            ins = nc.scalar.activation(v_win[:, cb], v[:, :, k0:k0 + KW], ACT.Copy)
                        ins.then_inc(S.v_ready, 1)
                if ph.kind == "hg":
                    act.wait_ge(S.unit_done, unit_of(ph, i, s) + 1)
                    bank = ps[:, [0, 1, 2, 0, 1][s], :]
                    if s == 0:
                        if not (isinstance(i, int) and i == 0):
                            act.wait_ge(S.ho_ready, i)
                        nc.scalar.activation(q_raw[:], bank, ACT.Copy)
                        nc.scalar.activation(q_sig[:], bank, ACT.Sigmoid).then_inc(S.ev_done, 1)
                    if s == 1:
                        nc.scalar.activation(v_raw[:], bank, ACT.Copy).then_inc(S.ev_done, 1)
                    if s in (2, 3):
                        nc.scalar.activation(f_sig[s - 2][:], bank, ACT.Sigmoid).then_inc(S.ev_done, 1)
                    if s == 4:
                        nc.scalar.activation(gt_raw[:], bank, ACT.Copy)
                        nc.scalar.activation(gt_sig[:], bank, ACT.Sigmoid).then_inc(S.ev_done, 1)

            def wait_heads(i):
                if not (isinstance(i, int) and i == 0):
                    act.wait_ge(S.s_mm, i * 2)

            def end(ph, i):
                if ph.kind == "na":
                    act.wait_ge(S.vkey_mm, i + 1)
                    if not (isinstance(i, int) and i == 0):
                        act.wait_ge(S.pv_mm, i * 2)
                    nc.scalar.activation(v_key[:], ps[:, 5:7, :], ACT.Copy).then_inc(S.vkey_ready, 1)
                    for hp in range(2):
                        head = i * 2 + hp
                        act.wait_ge(S.neg_done, head + 1)
                        for cb in range(CB):
                            ins = nc.scalar.activation(p_sb[hp][:, cb], p_sb[hp][:, cb], ACT.Exp,
                                                       bias=p_neg[hp][:, cb:cb + 1], accum_out=p_sum[hp][:, cb:cb + 1])
                        ins.then_inc(S.exp_done, 1)
                    act.wait_ge(S.pt_mm, i * 2 + 2)
                    nc.scalar.activation(p_key[1][:], ps[:, 5:7, :], ACT.Copy).then_inc(S.pt_ready1, 1)
                if ph.kind == "hg":
                    act.wait_ge(S.vtok_mm, i + 1)
                    nc.scalar.activation(v_tok[:], ps[:, 3, :], ACT.Copy).then_inc(S.vtok_ready, 1)
                    for d in range(2):
                        n = i * 2 + d
                        act.wait_ge(S.f_done, n + 1)
                        nc.scalar.activation(lg[d][:], f_sig[d][:], ACT.Ln).then_inc(S.lg_done, 1)
                    for d in range(2):
                        n = i * 2 + d
                        act.wait_ge(S.dd_done, n + 1)
                        nc.scalar.activation(e1[d][:], lg[d][:], ACT.Exp).then_inc(S.e1_done, 1)
                        nc.scalar.activation(lg[d][:], lg[d][:], ACT.Exp, scale=-1.0).then_inc(S.e2_done, 1)
                        act.wait_ge(S.gs2_done, n + 1)
                        lo = 1 - d
                        nc.scalar.activation(gam[d][:, lo:lo + NCH - 1], gam_t[d][:, lo:lo + NCH - 1], ACT.Exp).then_inc(S.gam_done, 1)
                    for d in range(2):
                        act.wait_ge(S.kkt_mm, i * 2 + d + 1)
                        nc.scalar.activation(kk_tok[d][:], ps[:, 3, :], ACT.Copy).then_inc(S.kkt_ready, 1)
                    act.wait_ge(S.inter_mm, i * 2 + 2)
                    nc.scalar.activation(v_raw[:], ps[:, 7, :], ACT.Square).then_inc(S.osq_done, 1)
                    act.wait_ge(S.ms_mm, i + 1)
                    nc.scalar.activation(q_sig[:], ps[:, 3, :], ACT.Ln, bias=eps_col[:]).then_inc(S.lnv_done, 1)
                    act.wait_ge(S.lnv_done, i + 1)
                    nc.scalar.activation(q_sig[:], q_sig[:], ACT.Exp, scale=-0.5).then_inc(S.hrstd_done, 1)

            def make_h(n):
                for k in range(KT):
                    act.wait_ge(S.norm_done, n * KT + k + 1)
                    if n * KT + k >= 2:
                        act.wait_ge(S.h_ready, n * KT + k - 1)
                    nc.scalar.activation(h32[k % 2][:], x[:, k, :], ACT.Identity, bias=B[:, n, k:k + 1], scale=A[:, n, k:k + 1])
                    nc.scalar.activation(h_hi[:, k, :], x[:, k, :], ACT.Identity, bias=B[:, n, k:k + 1],
                                         scale=A[:, n, k:k + 1]).then_inc(S.h_hi_done, 1)

            def after(ph):
                if ph.kind != "out" or not ph.last:
                    return
                n = ph.ln
                act.wait_ge(S.stat_done, 2 * n + 1)
                nc.scalar.activation(mean2[:], ps[:, 6, :], ACT.Square).then_inc(S.mean2_done, 1)
                act.wait_ge(S.var_done, n + 1)
                nc.scalar.activation(var[:], var[:], ACT.Sqrt).then_inc(S.sd_done, 1)
                if n < NLN - 1:
                    make_h(n + 1)
                else:
                    for k in range(KT):
                        act.wait_ge(S.norm_done, (n + 1) * KT + k + 1)
                        nc.scalar.activation(x[:, k, :], x[:, k, :], ACT.Identity, bias=AB[:, n, k:k + 1],
                                             scale=AG[:, n, k:k + 1]).then_inc(S.fin_done, 1)
                    for t in range(T // P):
                        act.wait_ge(S.fin_mm, 2 * t + 1)
                        nc.scalar.activation(x_tok[:, t, 0:D // 2], ps[:, 2 * t, :], ACT.Copy).then_inc(S.fin_left, 1)

            act.wait_ge(S.vec_done, 1)
            nc.scalar.activation(c_silu[:], ps[:, 6, 2 * P + 40:2 * P + 48], ACT.Silu).then_inc(S.silu_c, 1)
            for k in range(KT):
                act.wait_ge(S.xt_mm, k + 1)
                nc.scalar.activation(x[:, k, :], ps[:, k % 6, :], ACT.Copy, scale=ALPHA).then_inc(S.xt_done, 1)
            act.wait_ge(S.lb_act, 1)
            nc.scalar.activation(small[:, 0], small[:, 0], ACT.Exp)
            nc.scalar.activation(small[:, 1], small[:, 1], ACT.Exp).then_inc(S.lb_act, 1)
            for s in range(4):
                convert(phases[0], 0, s)
            make_h(0)
            drive(act, convert, finish, end, after)

        @block.vector
        def _(dve):
            count = {"cols": 0}

            def col(ins):
                count["cols"] += 1
                ins.then_inc(S.cols, 1)
                dve.wait_ge(S.cols, count["cols"])

            def convert(ph, i, s):
                dve.wait_ge(S.w_hi_done, unit_of(ph, i, s) + 1)
                nc.vector.tensor_tensor(w_lo[s][:, 0:ph.kt, :], raw[s][:, 0:ph.kt, :], w_hi[s][:, 0:ph.kt, :].bitcast(F32),
                                        ALU.subtract).then_inc(S.w_lo_done, 1)

            def finish(ph, i, s):
                if ph.kind == "in" and s % 2 == 1:
                    par = s // 2
                    pair = i * 2 + par + ph.p0
                    dve.wait_ge(S.silu_done, pair + 1)
                    nc.vector.tensor_tensor(g32[par][:], s_tmp[par][:], ps[:, s, :], ALU.mult).then_inc(S.pair_free, 1)
                    dve.wait_ge(S.pair_free, pair + 3)
                    nc.vector.tensor_scalar(g_hi[:, bass.ds(i * 2 + par, 1)], g32[par][:], 1.0, None, ALU.mult).then_inc(S.g_hi_done, 1)
                    dve.wait_ge(S.g_hi_done, pair + 1)
                    nc.vector.tensor_tensor(g_lo[:, bass.ds(i * 2 + par, 1)], g32[par][:],
                                            g_hi[:, bass.ds(i * 2 + par, 1)].bitcast(F32), ALU.subtract).then_inc(S.g_ready, 1)
                if ph.kind == "out" and s % ph.per_tile == ph.per_tile - 1:
                    j = s // ph.per_tile
                    tile = i * (ph.body // ph.per_tile) + j
                    dve.wait_ge(S.unit_done, unit_of(ph, i, s) + 1)
                    m = M[:, ph.ln, :]
                    xo = x[:, bass.ds(tile, 1)]
                    if not ph.last:
                        if ph.ln > 0:
                            dve.wait_ge(S.x_ready, KT * ph.ln)
                        nc.vector.scalar_tensor_tensor(out=xo, in0=ps[:, 4 + j % 2, :], scalar=m[:, bass.ds(tile, 1)], in1=xo,
                                                       op0=ALU.mult, op1=ALU.add).then_inc(S.y_read, 1)
                    else:
                        if ph.ffn is None:
                            dve.wait_ge(S.x_ready, KT * ph.ln)
                        else:
                            dve.wait_ge(S.y_read, ph.y0 + 2)
                        dve.wait_ge(S.qsum_done, tile + ph.t0 + 1)
                        nc.vector.scalar_tensor_tensor(out=zt[j % 2][:], in0=ps[:, 4 + j % 2, :], scalar=m[:, bass.ds(tile, 1)],
                                                       in1=xo, op0=ALU.mult, op1=ALU.add).then_inc(S.y_read, 1)
                        dve.wait_ge(S.y_read, tile + ph.y0 + 3)
                        nc.vector.tensor_scalar(xo, zt[j % 2][:], 1.0, None, ALU.mult).then_inc(S.x_copied, 1)
                if ph.kind == "na" and s == 1:
                    dve.wait_ge(S.unit_done, unit_of(ph, i, s) + 1)
                    if not (isinstance(i, int) and i == 0):
                        dve.wait_ge(S.s_mm, i * 2)
                    nc.vector.tensor_copy(k_sb[:].rearrange("p a b -> p (a b)"), ps[:, 1, :]).then_inc(S.k_ready, 1)

            def end(ph, i):
                if ph.kind == "na":
                    for hp in range(2):
                        head = i * 2 + hp
                        dve.wait_ge(S.s_mm, head + 1)
                        dve.wait_ge(S.bias_done, head + 1)
                        dve.wait_ge(S.pt_mm, i * 2)
                        nc.vector.memset(gate[:, hp:hp + 1], 0.0)
                        for cb in range(CB):
                            ins = nc.vector.tensor_tensor_reduce(
                                out=p_sb[hp][:, cb], in0=ps[:, 3 + cb // 2, (cb % 2) * KEYS:(cb % 2 + 1) * KEYS],
                                in1=bias[hp][:, VARIANT[cb]], scale=1.0, scalar=NEG, op0=ALU.add, op1=ALU.max,
                                accum_out=p_max[hp][:, cb:cb + 1])
                        ins.then_inc(S.bias_add, 1)
                        dve.wait_ge(S.bias_add, head + 1)
                        nc.vector.tensor_scalar(p_neg[hp][:], p_max[hp][:], -1.0, None, ALU.mult).then_inc(S.neg_done, 1)
                    for hp in range(2):
                        head = i * 2 + hp
                        dve.wait_ge(S.exp_done, head + 1)
                        nc.vector.reciprocal(p_inv[hp][:], p_sum[hp][:]).then_inc(S.inv_done, 1)
                        dve.wait_ge(S.inv_done, head + 1)
                        for cb in range(CB):
                            ins = nc.vector.tensor_scalar(p_sb[hp][:, cb], p_sb[hp][:, cb], p_inv[hp][:, cb:cb + 1], None, ALU.mult)
                        ins.then_inc(S.p_ready, 1)
                        if hp == 0:
                            dve.wait_ge(S.pt_mm, head + 1)
                            nc.vector.tensor_copy(p_key[0][:].rearrange("p a b -> p (a b)"),
                                                  ps[:, 5:7, :].rearrange("p a b -> p (a b)")).then_inc(S.pt_ready0, 1)
                    dve.wait_ge(S.pv_mm, i * 2 + 2)
                    nc.vector.tensor_copy(zt[0][:].rearrange("p (r c) -> p c r", r=ROWS),
                                          ps[:, 7, ::-1].rearrange("p (c r) -> p c r", r=ROWS)).then_inc(S.o_copied, 1)
                    dve.wait_ge(S.o_copied, i + 1)
                    nc.vector.tensor_scalar(ona_hi[:, bass.ds(i, 1)], zt[0][:], 1.0, None, ALU.mult).then_inc(S.o_hi_done, 1)
                    dve.wait_ge(S.o_hi_done, i + 1)
                    nc.vector.tensor_tensor(ona_lo[:, bass.ds(i, 1)], zt[0][:], ona_hi[:, bass.ds(i, 1)].bitcast(F32),
                                            ALU.subtract).then_inc(S.o_ready, 1)
                if ph.kind == "hg":
                    hgrn_end(ph, i)

            def hgrn_end(ph, i):
                chunked = [lambda a: a.rearrange("p (c t) -> p c t", t=CH)] * 2
                for d in range(2):
                    n = i * 2 + d
                    dve.wait_ge(S.ev_done, i * 5 + 3 + d)
                    nc.vector.tensor_scalar(f_sig[d][:], f_sig[d][:], lb1[:, d, bass.ds(i, 1)], lb[:, d, bass.ds(i, 1)],
                                            ALU.mult, ALU.add).then_inc(S.f_done, 1)
                    dve.wait_ge(S.f_done, n + 1)
                    nc.vector.tensor_scalar(kk[d][:], f_sig[d][:], -1.0, 1.0, ALU.mult, ALU.add).then_inc(S.k1_done, 1)
                for d in range(2):
                    n = i * 2 + d
                    step = 1 - 2 * d
                    dve.wait_ge(S.am_zero, 3)
                    dve.wait_ge(S.lg_done, n + 1)
                    if not (isinstance(i, int) and i == 0):
                        dve.wait_ge(S.inter_mm, i * 2)
                    nc.vector.tensor_tensor_scan(out=cum[d][:, ::step], data0=keep[d][:, ::step], data1=lg[d][:, ::step],
                                                 initial=0.0, op0=ALU.mult, op1=ALU.add).then_inc(S.cum_done, 1)
                    dve.wait_ge(S.cum_done, n + 1)
                    b = cum[d][:].rearrange("p (c t) -> p c t", t=CH)
                    ref = CH // 2 - d
                    last = (CH - 1) * (1 - d)
                    nc.vector.tensor_tensor(lg[d][:].rearrange("p (c t) -> p c t", t=CH), b,
                                            b[:, :, ref:ref + 1].to_broadcast([P, NCH, CH]), ALU.subtract).then_inc(S.dd_done, 1)
                    lo = 1 - d
                    fro = d
                    nxt = b[:, lo:lo + NCH - 1, ref:ref + 1].rearrange("p a b -> p (a b)")
                    end_ = b[:, fro:fro + NCH - 1, last:last + 1].rearrange("p a b -> p (a b)")
                    mine = b[:, fro:fro + NCH - 1, ref:ref + 1].rearrange("p a b -> p (a b)")
                    g = gam_t[d][:, lo:lo + NCH - 1]
                    nc.vector.tensor_tensor(g, end_, mine, ALU.subtract).then_inc(S.gs1_done, 1)
                    dve.wait_ge(S.gs1_done, n + 1)
                    nc.vector.tensor_tensor(g, g, nxt, ALU.add).then_inc(S.gs2_done, 1)
                for d in range(2):
                    n = i * 2 + d
                    dve.wait_ge(S.e1_done, n + 1)
                    dve.wait_ge(S.qs_done, i + 1)
                    nc.vector.tensor_tensor(e1[d][:], q_raw[:], e1[d][:], ALU.mult).then_inc(S.qq_done, 1)
                    dve.wait_ge(S.k1_done, n + 1)
                    dve.wait_ge(S.e2_done, n + 1)
                    nc.vector.tensor_tensor(kk[d][:], kk[d][:], lg[d][:], ALU.mult).then_inc(S.kk_done, 1)
                for d in range(2):
                    n = i * 2 + d
                    dve.wait_ge(S.am_zero, 3)
                    dve.wait_ge(S.a_mm, n + 1)
                    if not (isinstance(i, int) and i == 0):
                        dve.wait_ge(S.inter_mm, i * 2)
                    nc.vector.copy_predicated(am[d][:].rearrange("p (a b) -> p a b", b=P),
                                              tri[d][:].rearrange("p (a b) -> p a b", a=1).to_broadcast([P, T // P, P]),
                                              ps[:, 4, :].rearrange("p (a b) -> p a b", b=P)).then_inc(S.am_ready, 1)
                for d in range(2):
                    n = i * 2 + d
                    dve.wait_ge(S.pp_mm, n + 1)
                    dve.wait_ge(S.gam_done, n + 1)
                    order = list(range(NCH))[::1 - 2 * d]
                    for m, ch in enumerate(order[:-1]):
                        new = ps[:, 5 + ch % 2, (ch // 2) * P:(ch // 2 + 1) * P]
                        if m == 0:
                            nc.vector.tensor_copy(st[d][:, m], new).then_inc(S.st_done, 1)
                        else:
                            dve.wait_ge(S.st_done, n * (NCH - 1) + m)
                            nc.vector.scalar_tensor_tensor(out=st[d][:, m], in0=st[d][:, m - 1], scalar=gam[d][:, ch:ch + 1],
                                                           in1=new, op0=ALU.mult, op1=ALU.add).then_inc(S.st_done, 1)
                dve.wait_ge(S.hrstd_done, i + 1)
                nc.vector.tensor_tensor(q_raw[:], ps[:, 7, :], q_sig[:], ALU.mult).then_inc(S.n1_done, 1)
                dve.wait_ge(S.n1_done, i + 1)
                dve.wait_ge(S.gs_done, i + 1)
                nc.vector.scalar_tensor_tensor(out=gt_raw[:], in0=q_raw[:], scalar=vec[:, 2, bass.ds(i, 1)], in1=gt_raw[:],
                                               op0=ALU.mult, op1=ALU.mult).then_inc(S.n2_done, 1)
                dve.wait_ge(S.n2_done, i + 1)
                nc.vector.tensor_scalar(ohg_hi[:, bass.ds(i, 1)], gt_raw[:], 1.0, None, ALU.mult).then_inc(S.hhi_done, 1)
                dve.wait_ge(S.hhi_done, i + 1)
                nc.vector.tensor_tensor(ohg_lo[:, bass.ds(i, 1)], gt_raw[:], ohg_hi[:, bass.ds(i, 1)].bitcast(F32),
                                        ALU.subtract).then_inc(S.ho_ready, 1)

            def ada_steps(slot, k, w, arrived):
                dve.wait_ge(*arrived)
                if k == 0:
                    if not (isinstance(slot, int) and slot == 0):
                        dve.wait_ge(S.acc_out_ready, slot)
                    nc.vector.tensor_scalar(acc[:], w, c_silu[:, 0:1], None, ALU.mult).then_inc(S.ada_step, 1)
                else:
                    dve.wait_ge(S.ada_step, slot * 8 + k)
                    nc.vector.scalar_tensor_tensor(out=acc[:], in0=w, scalar=c_silu[:, k:k + 1], in1=acc[:],
                                                   op0=ALU.mult, op1=ALU.add).then_inc(S.ada_step, 1)
                if k == KT - 1:
                    dve.wait_ge(S.ada_step, slot * 8 + 8)
                    if not (isinstance(slot, int) and slot == 0):
                        dve.wait_ge(S.ada_reduced, slot)
                    nc.vector.tensor_copy(acc_out[:], acc[:]).then_inc(S.acc_out_ready, 1)

            def ride_ada(ph, i, s):
                for k in (2 * s, 2 * s + 1):
                    slot = i + ph.ada.slot0
                    uses = (slot - 2) * 4 + k // 2 + 1
                    ada_steps(slot, k, ada_raw[k % 2][:], (S.ada_loaded[k % 2], uses * 16))

            def take_mods(slot, many, layer, m):
                o = mods[:, layer, m:m + many].rearrange("p a b -> p (a b)")
                dve.wait_ge(S.ada_reduced, slot + many)
                col(nc.vector.tensor_tensor(o, ps[:, 7, slot * KT:(slot + many) * KT],
                                            vec[:, layer, m * KT:(m + many) * KT], ALU.add))

            def columns(n, layer, sub):
                g = vec[:, 0, 72 + (n - 1) * KT:72 + n * KT]
                b = vec[:, 1, 72 + (n - 1) * KT:72 + n * KT]
                sc = mods[:, layer, 3 * sub + 1]
                sh = mods[:, layer, 3 * sub]
                t = small[:, 2, 0:KT]
                col(nc.vector.tensor_scalar(t, sc, 1.0, None, ALU.add))
                col(nc.vector.tensor_tensor(A[:, n], g, t, ALU.mult))
                col(nc.vector.tensor_tensor(t, b, t, ALU.mult))
                col(nc.vector.tensor_tensor(B[:, n], t, sh, ALU.add))

            def scale(n, layer, sub):
                col(nc.vector.tensor_scalar(M[:, n], mods[:, layer, 3 * sub + 2], 1.0 if sub == 1 else 0.5, None, ALU.mult))

            def low_parts(n, k):
                dve.wait_ge(S.h_hi_done, n * KT + k + 1)
                nc.vector.tensor_tensor(h_lo[:, k, :], h32[k % 2][:], h_hi[:, k, :].bitcast(F32), ALU.subtract).then_inc(S.h_ready, 1)

            def after(ph):
                if ph.ada is not None:
                    if ph.n == 0:
                        take_mods(2, 6, 0, 2)
                        scale(0, 0, 0)
                        columns(1, 0, 1)
                        scale(1, 0, 1)
                        columns(2, 0, 2)
                    if ph.n == 2:
                        dve.wait_ge(S.ada_reduced, 13)
                        take_mods(8, 4, 1, 0)
                        take_mods(12, 1, 0, 8)
                        scale(2, 0, 2)
                        columns(3, 1, 0)
                        scale(3, 1, 0)
                    if ph.n == 8:
                        take_mods(13, 5, 1, 4)
                        columns(4, 1, 1)
                        scale(4, 1, 1)
                        columns(5, 1, 2)
                        scale(5, 1, 2)
                if ph.kind != "out" or not ph.last:
                    return
                n = ph.ln
                dve.wait_ge(S.mean2_done, n + 1)
                dve.wait_ge(S.stat_done, 2 * n + 2)
                nc.vector.scalar_tensor_tensor(out=var[:], in0=mean2[:], scalar=-1.0, in1=ps[:, 7, :],
                                               op0=ALU.mult, op1=ALU.add).then_inc(S.var1_done, 1)
                dve.wait_ge(S.var1_done, n + 1)
                nc.vector.tensor_scalar(var[:], var[:], 0.0, EPS, ALU.max, ALU.add).then_inc(S.var_done, 1)

                def centre(k):
                    if k == 0:
                        dve.wait_ge(S.x_copied, KT * (n + 1))
                    nc.vector.tensor_tensor(x[:, k, :], x[:, k, :], ps[:, 6, :], ALU.subtract).then_inc(S.cent_done, 1)

                for k in range(3):
                    centre(k)
                dve.wait_ge(S.sd_done, n + 1)
                nc.vector.reciprocal(rstd[:], var[:]).then_inc(S.rstd_done, 1)
                dve.wait_ge(S.rstd_done, n + 1)
                for k in range(KT):
                    if k >= 3:
                        centre(k)
                    dve.wait_ge(S.cent_done, KT * n + k + 1)
                    nc.vector.tensor_tensor(x[:, k, :], x[:, k, :], rstd[:], ALU.mult).then_inc(S.norm_done, 1)
                    if k >= 1 and n < NLN - 1:
                        low_parts(n + 1, k - 1)
                if n < NLN - 1:
                    low_parts(n + 1, KT - 1)
                else:
                    for t in range(T // P):
                        dve.wait_ge(S.fin_mm, 2 * t + 2)
                        nc.vector.tensor_copy(x_tok[:, t, D // 2:D], ps[:, 2 * t + 1, :]).then_inc(S.fin_right, 1)

            nc.vector.memset(one[:], 1.0).then_inc(S.const_done, 1)
            nc.vector.memset(eps_col[:], EPS).then_inc(S.const_done, 1)
            nc.vector.memset(mean_w[:], 1.0 / D).then_inc(S.pair_free, 2)
            nc.vector.memset(head_w[:], 1.0 / P).then_inc(S.y_read, 2)
            dve.wait_ge(S.vec_mm, 1)
            for t, cols in enumerate((120, 120, 48)):
                ins = nc.vector.tensor_copy(vec[:, t, 0:cols], ps[:, 6, t * P:t * P + cols])
            ins.then_inc(S.vec_done, 1)
            dve.wait_ge(S.vec_done, 1)
            for dr in range(2):
                l0 = vec[:, 2, 8 + dr * 16:16 + dr * 16]
                l1 = vec[:, 2, 16 + dr * 16:24 + dr * 16]
                mx = small[:, 2, 0:KT]
                col(nc.vector.tensor_tensor(mx, l0, l1, ALU.max))
                col(nc.vector.tensor_tensor(small[:, 0, dr * KT:(dr + 1) * KT], l0, mx, ALU.subtract))
                col(nc.vector.tensor_tensor(small[:, 1, dr * KT:(dr + 1) * KT], l1, mx, ALU.subtract))
            nc.vector.tensor_scalar(AG[:], vec[:, 0, 72:120].rearrange("p (a b) -> p a b", b=KT), ALPHA, None, ALU.mult).then_inc(S.lb_act, 1)
            col(nc.vector.tensor_scalar(AB[:], vec[:, 1, 72:120].rearrange("p (a b) -> p a b", b=KT), ALPHA, None, ALU.mult))
            col(nc.vector.tensor_copy(AG[:, NLN - 1], vec[:, 0, 112:120]))
            col(nc.vector.tensor_copy(AB[:, NLN - 1], vec[:, 1, 112:120]))
            dve.wait_ge(S.silu_c, 1)
            for m in range(2):
                for k in range(KT):
                    g = m * KT + k
                    ada_steps(m, k, boot[g % 7][:], (S.boot_loaded[g % 7], 16 * (g // 7 + 1)))
            dve.wait_ge(S.lb_act, 2)
            col(nc.vector.tensor_tensor(small[:, 2], small[:, 0], small[:, 1], ALU.add))
            col(nc.vector.reciprocal(small[:, 3], small[:, 2]))
            col(nc.vector.tensor_tensor(lb[:].rearrange("p a b -> p (a b)"), small[:, 1], small[:, 3], ALU.mult))
            col(nc.vector.tensor_scalar(lb1[:], lb[:], -1.0, 1.0, ALU.mult, ALU.add))
            for s in range(4):
                convert(phases[0], 0, s)
            take_mods(0, 2, 0, 0)
            col(nc.vector.tensor_scalar(A[:, 0], mods[:, 0, 1], 1.0, 1.0 / ALPHA, ALU.add, ALU.mult))
            dve.wait_ge(S.xt_done, KT)
            nc.vector.tensor_copy(B[:, 0], mods[:, 0, 0]).then_inc(S.norm_done, KT)
            for k in range(KT):
                low_parts(0, k)
            for s in range(4):
                ride_ada(phases[0], 0, s)
            drive(dve, convert, finish, end, after, ride_ada)

        @block.gpsimd
        def _(pool):
            nc.gpsimd.memset(ident[:], 0.0).then_inc(S.hconst, 1)
            pool.wait_ge(S.hconst, 1)
            nc.gpsimd.affine_select(out=ident[:], in_=ident[:], compare_op=ALU.not_equal, fill=1.0, base=0,
                                    pattern=[[-1, P]], channel_multiplier=1).then_inc(S.const_done, 1)
            nc.gpsimd.memset(zsum[:], 0.0).then_inc(S.tab_zero, 1)

            def restart_sums(n):
                if n > 0:
                    pool.wait_ge(S.stat_done, 2 * n)
                else:
                    pool.wait_ge(S.tab_init, 16)
                nc.gpsimd.memset(zsum[:], 0.0).then_inc(S.zeroed, 1)
                nc.gpsimd.memset(qsum[:], 0.0).then_inc(S.zeroed, 1)
                pool.wait_ge(S.zeroed, 2 * (n + 1))

            def next_residual(n):
                for k in range(KT):
                    pool.wait_ge(S.h_hi_done, (n + 1) * KT + k + 1)
                    nc.gpsimd.tensor_scalar(x[:, k, :], x[:, k, :], AG[:, n, k:k + 1], AB[:, n, k:k + 1],
                                            ALU.mult, ALU.add).then_inc(S.x_ready, 1)

            def add_up(ph, i, j, tiles):
                tile = i * tiles + j
                pool.wait_ge(S.y_read, tile + ph.y0 + 3)
                pool.wait_ge(S.zsum_done, tile + ph.t0 + 1)
                nc.gpsimd.tensor_tensor(zsum[:], zsum[:], zt[j % 2][:], ALU.add).then_inc(S.zsum_done, 1)
                pool.wait_ge(S.sq_done, tile + ph.t0 + 1)
                nc.gpsimd.tensor_tensor(qsum[:], qsum[:], sq[:], ALU.add).then_inc(S.qsum_done, 1)

            def make_bias(i):
                for hp in range(2):
                    head = i * 2 + hp
                    pool.wait_ge(S.tab_loaded[hp], i * 16 + 16)
                    if not (isinstance(i, int) and i == 0):
                        pool.wait_ge(S.bias_add, head - 1)
                    for v in range(3):
                        ins = nc.gpsimd.tensor_tensor(bias[hp][:, v].rearrange("p (a b) -> p a b", b=KW),
                                                      tab[hp][:, :, SHIFT[v]:SHIFT[v] + KW], mask[:, v], ALU.add)
                    ins.then_inc(S.bias_done, 1)

            def make_mask():
                nc.gpsimd.memset(mask[:], 0.0).then_inc(S.mask_done, 1)
                tests = [(0, 0, KW, 8, -1, 71), (0, QB, KW, -8, 1, 56),
                         (1, 0, KW, 8, -1, 7), (1, 0, KW, -8, 1, 120),
                         (2, 0, QB, 8, -1, -57), (2, 0, KW, -8, 1, 184)]
                for n, (v, j0, j1, step, chan, base) in enumerate(tests):
                    pool.wait_ge(S.mask_done, n + 1)
                    part = mask[:, v, :, j0:j1]
                    nc.gpsimd.affine_select(out=part, in_=part, compare_op=ALU.is_ge, fill=NEG, base=base + step * j0 + (P - 1) * chan,
                                            pattern=[[0, ROWS], [step, j1 - j0]], channel_multiplier=-chan).then_inc(S.mask_done, 1)
                pool.wait_ge(S.mask_done, len(tests) + 1)

            def hgrn_constants():
                for d in range(2):
                    nc.gpsimd.memset(am[d][:], 0.0).then_inc(S.am_zero, 1)
                    nc.gpsimd.memset(keep[d][:], 1.0).then_inc(S.hconst, 1)
                pool.wait_ge(S.hconst, 3)
                for d in range(2):
                    first = (CH - 1) * d
                    nc.gpsimd.memset(keep[d][:].rearrange("p (c t) -> p c t", t=CH)[:, :, first:first + 1], 0.0).then_inc(S.hconst, 1)
                done = 5
                for d in range(2):
                    nc.gpsimd.memset(tri_f[:], 1.0).then_inc(S.hconst, 1)
                    done += 1
                    pool.wait_ge(S.hconst, done)
                    nc.gpsimd.affine_select(out=tri_f[:], in_=tri_f[:], compare_op=ALU.is_ge, fill=0.0, base=0,
                                            pattern=[[1 - 2 * d, P]], channel_multiplier=2 * d - 1).then_inc(S.hconst, 1)
                    done += 1
                    pool.wait_ge(S.hconst, done)
                    if d == 0:
                        nc.gpsimd.affine_select(out=tri_f[:, CH:P], in_=tri_f[:, CH:P], compare_op=ALU.is_ge, fill=0.0, base=-CH,
                                                pattern=[[0, CH]], channel_multiplier=1).then_inc(S.hconst, 1)
                    else:
                        nc.gpsimd.affine_select(out=tri_f[:, 0:CH], in_=tri_f[:, 0:CH], compare_op=ALU.is_ge, fill=0.0, base=CH - 1,
                                                pattern=[[0, CH]], channel_multiplier=-1).then_inc(S.hconst, 1)
                    done += 1
                    pool.wait_ge(S.hconst, done)
                    nc.gpsimd.tensor_copy(tri[d][:], tri_f[:]).then_inc(S.hconst, 1)
                    done += 1
                    pool.wait_ge(S.hconst, done)
                nc.gpsimd.memset(tri_f[:, 0:1], 0.0).then_inc(S.am_zero, 1)

            def gates(i):
                pool.wait_ge(S.ev_done, i * 5 + 1)
                nc.gpsimd.tensor_tensor(q_raw[:], q_raw[:], q_sig[:], ALU.mult).then_inc(S.qs_done, 1)
                pool.wait_ge(S.ev_done, i * 5 + 5)
                nc.gpsimd.tensor_tensor(gt_raw[:], gt_raw[:], gt_sig[:], ALU.mult).then_inc(S.gs_done, 1)
                for d in range(2):
                    n = i * 2 + d
                    lo = 1 - d
                    pool.wait_ge(S.qq_done, n + 1)
                    pool.wait_ge(S.gam_done, n + 1)
                    pool.wait_ge(S.gs2_done, n + 1)
                    part = lambda a: a.rearrange("p (c t) -> p c t", t=CH)[:, lo:lo + NCH - 1]
                    nc.gpsimd.tensor_tensor(part(cum[d][:]), part(e1[d][:]),
                                            gam[d][:, lo:lo + NCH - 1].rearrange("p (a b) -> p a b", b=1).to_broadcast([P, NCH - 1, CH]),
                                            ALU.mult).then_inc(S.qg_done, 1)

            first = True
            for ph in phases:
                if ph.kind == "na":
                    pool.wait_ge(S.unit_done, ph.u0)
                    make_mask()
                    make_bias(0)
                    with pool.Fori(1, ph.iters) as i:
                        make_bias(i)
                if ph.kind == "hg":
                    pool.wait_ge(S.unit_done, ph.u0)
                    hgrn_constants()
                    with pool.Fori(0, ph.iters) as i:
                        gates(i)
                if ph.kind == "out" and ph.last:
                    if first:
                        restart_sums(0)
                        nc.gpsimd.memset(sq[:], 0.0).then_inc(S.qsum_done, 2)
                        nc.gpsimd.memset(qsum[:], 0.0).then_inc(S.zsum_done, 1)
                        pool.wait_ge(S.zsum_done, 1)
                        first = False
                    else:
                        restart_sums(ph.ln)
                    tiles = ph.body // ph.per_tile
                    with pool.Fori(0, ph.iters) as i:
                        for j in range(tiles):
                            add_up(ph, i, j, tiles)
                    if ph.ln < NLN - 1:
                        next_residual(ph.ln)


        @block.tensor
        def _(pe):
            def unit(ph, i, s, bank, hi, lo, first, start, stop, ready=None, at0=0):
                pe.wait_ge(S.w_lo_done, unit_of(ph, i, s) + 1)
                for k in range(ph.kt):
                    if ready is not None:
                        pe.wait_ge(ready[0], ready[1] + k + 1)
                    a, b = hi[:, at0 + k, :], lo[:, at0 + k, :]
                    nc.tensor.matmul(ps[:, bank, :], w_hi[s][:, k, :], a, start=start and k == 0, stop=False)
                    nc.tensor.matmul(ps[:, bank, :], w_hi[s][:, k, :], b, start=False, stop=False)
                    ins = nc.tensor.matmul(ps[:, bank, :], w_lo[s][:, k, :], a, start=False, stop=stop and k == ph.kt - 1)
                ins.then_inc(S.unit_done, 1)

            def reduce_ada(slot):
                pe.wait_ge(S.acc_out_ready, slot + 1)
                for k in range(KT):
                    ins = nc.tensor.matmul(ps[:, 7, bass.ds(slot * KT + k, 1)], acc_out[:, k * P:(k + 1) * P], one[:], start=True, stop=True)
                ins.then_inc(S.ada_reduced, 1)

            def attend(i, part):
                if part == 0:
                    pe.wait_ge(S.v_ready, i + 1)
                    if not (isinstance(i, int) and i == 0):
                        pe.wait_ge(S.pt_ready1, i)
                    for w in range(CB * 2):
                        src = v_win[:, w // 2].rearrange("p a b -> p (a b)")[:, (w % 2) * P:(w % 2 + 1) * P]
                        ins = nc.tensor.transpose(ps[:, 5 + w // 4, (w % 4) * P:(w % 4 + 1) * P], src, ident[:])
                    ins.then_inc(S.vkey_mm, 1)
                    pe.wait_ge(S.q_ready, i + 1)
                    pe.wait_ge(S.k_ready, i + 1)
                    scores(i, 0)
                if part == 1:
                    scores(i, 1)
                    turn(i, 0)
                if part == 2:
                    turn(i, 1)
                    values(i, 0)
                    values(i, 1)

            def scores(i, hp):
                head = i * 2 + hp
                if hp == 1 or not (isinstance(i, int) and i == 0):
                    pe.wait_ge(S.bias_add, head)
                r = slice(64 * hp, 64 * hp + 64)
                q = q_sb[:].rearrange("p a b -> p (a b)")
                for cb in range(CB):
                    k0 = KEY_START[cb]
                    ins = nc.tensor.matmul(ps[:, 3 + cb // 2, (cb % 2) * KEYS:(cb % 2 + 1) * KEYS], q[r, (CB - 1 - cb) * P:(CB - cb) * P],
                                           k_sb[r, :, k0:k0 + KW], start=True, stop=True)
                ins.then_inc(S.s_mm, 1)

            def turn(i, hp):
                pe.wait_ge(S.p_ready, i * 2 + hp + 1)
                if hp == 0:
                    pe.wait_ge(S.vkey_ready, i + 1)
                else:
                    pe.wait_ge(S.pt_ready0, i + 1)
                for w in range(CB * 2):
                    ins = nc.tensor.transpose(ps[:, 5 + w // 4, (w % 4) * P:(w % 4 + 1) * P],
                                              p_sb[hp][:, w // 2, (w % 2) * P:(w % 2 + 1) * P], ident[:])
                ins.then_inc(S.pt_mm, 1)

            def values(i, hp):
                if hp == 0:
                    if not (isinstance(i, int) and i == 0):
                        pe.wait_ge(S.o_copied, i)
                    pe.wait_ge(S.pt_ready0, i + 1)
                else:
                    pe.wait_ge(S.pt_ready1, i + 1)
                r = slice(64 * hp, 64 * hp + 64)
                for w in range(CB * 2):
                    cb = w // 2
                    ins = nc.tensor.matmul(ps[r, 7, (CB - 1 - cb) * P:(CB - cb) * P], v_key[:, w, r], p_key[hp][:, w, :],
                                           start=w % 2 == 0, stop=w % 2 == 1)
                ins.then_inc(S.pv_mm, 1)

            def hgrn(i, part):
                first = isinstance(i, int) and i == 0
                if part == 0:
                    pe.wait_ge(S.ev_done, i * 5 + 2)
                    if first:
                        pe.wait_ge(S.const_done, 3)
                    else:
                        pe.wait_ge(S.lnv_done, i)
                    for b in range(T // P):
                        ins = nc.tensor.transpose(ps[:, 3, b * P:(b + 1) * P], v_raw[:, b * P:(b + 1) * P], ident[:])
                    ins.then_inc(S.vtok_mm, 1)
                if part in (1, 2):
                    d = part - 1
                    n = i * 2 + d
                    pe.wait_ge(S.kk_done, n + 1)
                    pe.wait_ge(S.qq_done, n + 1)
                    if part == 2 or not first:
                        pe.wait_ge(S.am_ready, n)
                    half = CH // 2
                    for ch in range(NCH):
                        key0 = CH * (ch % 2)
                        col0 = P * (ch // 2)
                        early, late = (0, half) if d == 0 else (half, 0)
                        nc.tensor.matmul(ps[key0:key0 + CH, 4, col0 + key0 + late:col0 + key0 + late + half],
                                         kk[d][:, ch * CH:(ch + 1) * CH], e1[d][:, ch * CH + late:ch * CH + late + half],
                                         start=True, stop=True)
                        e = slice(ch * CH + early, ch * CH + early + half)
                        ins = nc.tensor.matmul(ps[key0 + early:key0 + early + half, 4, e], kk[d][:, e], e1[d][:, e],
                                               start=True, stop=True)
                    ins.then_inc(S.a_mm, 1)
                    if d == 0:
                        pe.wait_ge(S.vtok_ready, i + 1)
                    else:
                        pe.wait_ge(S.kkt_ready, n)
                    for b in range(T // P):
                        c = slice(b * P, (b + 1) * P)
                        ins = nc.tensor.transpose(ps[:, 3, c], kk[d][:, c], ident[:])
                    ins.then_inc(S.kkt_mm, 1)
                if part in (3, 4):
                    d = part - 3
                    n = i * 2 + d
                    pe.wait_ge(S.kkt_ready, n + 1)
                    if d == 1:
                        pe.wait_ge(S.st_done, n * (NCH - 1))
                    elif not first:
                        pe.wait_ge(S.st_done, n * (NCH - 1))
                    for ch in range(NCH):
                        r = slice(CH * (ch % 2), CH * (ch % 2 + 1))
                        c = slice((ch // 2) * P, (ch // 2 + 1) * P)
                        ins = nc.tensor.matmul(ps[:, 5 + ch % 2, (ch // 2) * P:(ch // 2 + 1) * P], kk_tok[d][r, c], v_tok[r, c],
                                               start=True, stop=True)
                    ins.then_inc(S.pp_mm, 1)
                if part == 4:
                    for d in range(2):
                        n = i * 2 + d
                        if d == 0 and not first:
                            pe.wait_ge(S.n1_done, i)
                        pe.wait_ge(S.am_ready, n + 1)
                        for b in range(T // P):
                            c = slice(b * P, (b + 1) * P)
                            nc.tensor.matmul(ps[:, 7, c], v_tok[:, c], am[d][:, c], start=d == 0 and b == 0, stop=False,
                                             skip_group_check=True)
                        pe.wait_ge(S.qg_done, n + 1)
                        order = list(range(NCH))[::1 - 2 * d]
                        for m, ch in enumerate(order[1:]):
                            pe.wait_ge(S.st_done, n * (NCH - 1) + m + 1)
                            ins = nc.tensor.matmul(ps[:, 7, ch * CH:(ch + 1) * CH], st[d][:, m], cum[d][:, ch * CH:(ch + 1) * CH],
                                                   start=False, stop=d == 1 and m == NCH - 2, skip_group_check=True)
                        ins.then_inc(S.inter_mm, 1)
                    pe.wait_ge(S.osq_done, i + 1)
                    nc.tensor.matmul(ps[:, 3, :], head_w[:], v_raw[:], start=True, stop=True).then_inc(S.ms_mm, 1)

            pe.wait_ge(S.const_done, 3)
            pe.wait_ge(S.small_in, 16 * 7)
            for t, rows in enumerate((120, 120, 48)):
                ins = nc.tensor.transpose(ps[:, 6, t * P:t * P + rows], vrow[0:rows, t, :], ident[0:rows, 0:rows])
            ins.then_inc(S.vec_mm, 1)
            pe.wait_ge(S.x_loaded, 16 * (T // P))
            for k in range(KT):
                if k >= 6:
                    pe.wait_ge(S.xt_done, k - 5)
                for t in range(T // P):
                    ins = nc.tensor.transpose(ps[:, k % 6, t * P:(t + 1) * P], x_tok[:, t, k * P:(k + 1) * P], ident[:])
                ins.then_inc(S.xt_mm, 1)
            reduce_ada(0)
            reduce_ada(1)

            h_uses = 0
            for ph in phases:
                if ph.kind == "in":
                    with pe.Fori(0, ph.iters) as i:
                        for s in range(4):
                            if s % 2 == 0:
                                pe.wait_ge(S.pair_free, i * 2 + (ph.p0 + s // 2 + 1))
                            ready = (S.h_ready, ph_h(ph) * KT) if s == 0 and ph.half == 0 else None
                            unit(ph, i, s, s, h_hi, h_lo, None, True, True, ready)
                        if ph.ada is not None:
                            reduce_ada(i + ph.ada.slot0)
                if ph.kind == "out":
                    if ph.ffn is None:
                        hi, lo = (ona_hi, ona_lo) if ph.mixer == "na" else (ohg_hi, ohg_lo)
                        ready = (S.o_ready, 0) if ph.mixer == "na" else (S.ho_ready, 0)
                    else:
                        hi, lo = g_hi, g_lo
                    with pe.Fori(0, ph.iters) as i:
                        for s in range(4):
                            j = s // ph.per_tile
                            if s % ph.per_tile == 0:
                                pe.wait_ge(S.y_read, i * (4 // ph.per_tile) + (ph.y0 + j + 1))
                            if ph.ffn is None:
                                unit(ph, i, s, 4 + j % 2, hi, lo, None, True, True, ready if s == 0 else None)
                            else:
                                a = (s % 2) * ph.kt
                                unit(ph, i, s, 4 + j % 2, hi, lo, None, s % 2 == 0, s % 2 == 1,
                                     (S.g_ready, a + g_base(ph)) if s < 2 else None, a)
                    if ph.last:
                        for n, (sem, src) in enumerate(((S.zsum_done, zsum), (S.qsum_done, qsum))):
                            pe.wait_ge(sem, ph.t0 + KT + 1 + n)
                            nc.tensor.matmul(ps[:, 6 + n, :], mean_w[:], src[:], start=True, stop=True).then_inc(S.stat_done, 1)
                if ph.kind == "na":
                    def proj(i, s):
                        if isinstance(i, int):
                            ready = (S.h_ready, KT) if s == 0 else None
                        else:
                            pe.wait_ge([S.q_ready, S.k_ready, S.v_ready][s], i)
                            ready = None
                        unit(ph, i, s, s, h_hi, h_lo, None, True, True, ready)
                    for s in range(3):
                        proj(0, s)
                    with pe.Fori(1, ph.iters) as i:
                        for s in range(3):
                            proj(i, s)
                            attend(i - 1, s)
                    for s in range(3):
                        attend(ph.iters - 1, s)
                if ph.kind == "hg":
                    banks = [0, 1, 2, 0, 1]

                    def proj(i, s):
                        u = i * 5 + s
                        if not isinstance(i, int) or s >= 3:
                            pe.wait_ge(S.ev_done, u - [1, 1, 4, 2, 2][s])
                        unit(ph, i, s, banks[s], h_hi, h_lo, None, True, True, (S.h_ready, 4 * KT) if isinstance(i, int) and s == 0 else None)
                    for s in range(5):
                        proj(0, s)
                    with pe.Fori(1, ph.iters) as i:
                        for s in range(3):
                            proj(i, s)
                            hgrn(i - 1, s)
                        hgrn(i - 1, 3)
                        hgrn(i - 1, 4)
                        proj(i, 3)
                        proj(i, 4)
                    for s in range(5):
                        hgrn(ph.iters - 1, s)
            for t in range(T // P):
                for half in range(2):
                    for k in range(4):
                        kt = half * 4 + k
                        if t == 0:
                            pe.wait_ge(S.fin_done, kt + 1)
                        ins = nc.tensor.transpose(ps[:, 2 * t + half, k * P:(k + 1) * P], x[:, kt, t * P:(t + 1) * P], ident[:])
                    ins.then_inc(S.fin_mm, 1)


_INS = ['x', 'c', 'ada_w', 'ada_b', 'ln_g', 'ln_b', 'ffn_w_in', 'ffn_w_out', 'na_w_qkv', 'na_rpb', 'na_w_out',
        'hgrn_w_in', 'hgrn_lb_logits', 'hgrn_norm_g', 'hgrn_w_out']
_OUTS = [((1, 512, 1024), 'float32')]


def kernel(**inputs):
    import numpy as _np
    import concourse.bacc as _bacc
    from concourse import mybir as _mybir
    from concourse.bass_utils import run_bass_kernel_spmd as _run

    nc = _bacc.Bacc("TRN2", target_bir_lowering=False, num_devices=1)
    arrays, args = {}, []
    for name in _INS:
        a = _np.ascontiguousarray(inputs[name])
        arrays[f"in_{name}_dram"] = a
        args.append(nc.dram_tensor(f"in_{name}_dram", a.shape, _mybir.dt.from_np(a.dtype), kind="ExternalInput").ap())
    for i, (shape, dtype) in enumerate(_OUTS):
        dt = _mybir.dt.from_np(_np.dtype(dtype))
        args.append(nc.dram_tensor(f"out_{i}_dram", shape, dt, kind="ExternalOutput").ap())
    build(nc, *args)
    r = _run(nc, [arrays], core_ids=[0])
    got = tuple(r.results[0][f"out_{i}_dram"] for i in range(len(_OUTS)))
    return got[0]
```
